# Optimizing a Trainium2 kernel written in Bass

```python
import math
import jax, jax.numpy as jnp
from jax import lax
import numpy as np

D_MODEL = 1024
BATCH = 1
SEQ = 512
DEPTH = 4

N_MIXERS = 3
N_ATTN_LAYERS = (DEPTH + 2) // 3
N_CONV_LAYERS = (DEPTH + 1) // 3
N_POOL_LAYERS = DEPTH // 3

N_HEADS = 8
HEAD_DIM = D_MODEL // N_HEADS // 2
ROT_DIM = HEAD_DIM // 4
ROPE_THETA = 500000.0
Q_BLOCK = 128
LAMBDA_STD = 0.1

CONV_WIDTH = 31

POOL_WINDOWS = (2, 4, 8, 16)
N_POOL_GROUPS = len(POOL_WINDOWS)
POOL_GROUP = D_MODEL // N_POOL_GROUPS

D_FF = int(math.ceil(8 * D_MODEL / 3 / 256) * 256)

ALPHA = float((2 * DEPTH) ** 0.25)
BETA = float((8 * DEPTH) ** -0.25)
LN_EPS = 1e-5

kernel_name = 'hybrid_diffattn_conformer_pool_deepnorm'

def _layer_norm(x, g, b):
    x32 = x.astype(jnp.float32)
    mu = jnp.mean(x32, axis=-1, keepdims=True)
    var = jnp.mean(jnp.square(x32 - mu), axis=-1, keepdims=True)
    y = (x32 - mu) * lax.rsqrt(var + LN_EPS) * g.astype(jnp.float32) + b.astype(jnp.float32)
    return y.astype(x.dtype)

def _rms_norm(x, g):
    x32 = x.astype(jnp.float32)
    y = x32 * lax.rsqrt(jnp.mean(jnp.square(x32), axis=-1, keepdims=True) + LN_EPS) * g.astype(jnp.float32)
    return y.astype(x.dtype)

def _rope_tables(seq, dtype):
    inv_freq = ROPE_THETA ** (-jnp.arange(0, ROT_DIM, 2, dtype=jnp.float32) / ROT_DIM)
    pos = jnp.arange(seq, dtype=jnp.float32)
    ang = pos[:, None] * inv_freq[None, :]
    return jnp.cos(ang).astype(dtype), jnp.sin(ang).astype(dtype)

def _partial_rope(x, cos, sin):
    half = ROT_DIM // 2
    c = cos[None, :, None, None, :]
    s = sin[None, :, None, None, :]
    x1 = x[..., :half]
    x2 = x[..., half:ROT_DIM]
    return jnp.concatenate([x1 * c - x2 * s, x2 * c + x1 * s, x[..., ROT_DIM:]], axis=-1)

def _diff_attention(x, wqkv, wo, lam, subln_g, cos, sin, lambda_init):
    B, S, _ = x.shape
    qkv = x @ wqkv
    q, k, v = jnp.split(qkv, 3, axis=-1)
    q = _partial_rope(q.reshape(B, S, N_HEADS, 2, HEAD_DIM), cos, sin)
    k = _partial_rope(k.reshape(B, S, N_HEADS, 2, HEAD_DIM), cos, sin)
    v = v.reshape(B, S, N_HEADS, 2 * HEAD_DIM)
    lam32 = lam.astype(jnp.float32)
    lam_full = (jnp.exp(jnp.sum(lam32[0] * lam32[1])) - jnp.exp(jnp.sum(lam32[2] * lam32[3]))
                + lambda_init)
    scale = HEAD_DIM ** -0.5
    n_blocks = S // Q_BLOCK
    q_blocks = q.reshape(B, n_blocks, Q_BLOCK, N_HEADS, 2, HEAD_DIM).transpose(1, 0, 2, 3, 4, 5)
    starts = jnp.arange(n_blocks, dtype=jnp.int32) * Q_BLOCK
    k_pos = jnp.arange(S, dtype=jnp.int32)

    def one_block(args):
        q_blk, start = args
        s = jnp.einsum('bqhmd,bkhmd->bhmqk', q_blk, k).astype(jnp.float32) * scale
        q_pos = start + jnp.arange(Q_BLOCK, dtype=jnp.int32)
        causal = k_pos[None, :] <= q_pos[:, None]
        s = jnp.where(causal, s, -1e30)
        p = jax.nn.softmax(s, axis=-1)
        a = p[:, :, 0] - lam_full * p[:, :, 1]
        return jnp.einsum('bhqk,bkhe->bqhe', a.astype(v.dtype), v)

    o = lax.map(one_block, (q_blocks, starts))
    o = o.transpose(1, 0, 2, 3, 4).reshape(B, S, N_HEADS, 2 * HEAD_DIM)
    o = _rms_norm(o, subln_g) * (1.0 - lambda_init)
    return o.reshape(B, S, N_HEADS * 2 * HEAD_DIM) @ wo

def _conformer_conv(x, pw1_w, pw1_b, dw_w, dw_b, ln_g, ln_b, pw2_w, pw2_b):
    h = x @ pw1_w + pw1_b
    a, gate = jnp.split(h, 2, axis=-1)
    h = a * jax.nn.sigmoid(gate)
    h = lax.conv_general_dilated(
        h, dw_w[:, None, :].astype(h.dtype), window_strides=(1,),
        padding=[(CONV_WIDTH - 1, 0)],
        dimension_numbers=('NWC', 'WIO', 'NWC'),
        feature_group_count=D_MODEL) + dw_b
    h = jax.nn.silu(_layer_norm(h, ln_g, ln_b))
    return h @ pw2_w + pw2_b

def _multiscale_pool(x, pool_w, pool_b, pool_scale):
    B, S, D = x.shape
    x32 = x.astype(jnp.float32)
    csum = jnp.concatenate([jnp.zeros((B, 1, D), jnp.float32), jnp.cumsum(x32, axis=1)], axis=1)
    t_idx = jnp.arange(S, dtype=jnp.int32)
    outs = []
    for g, w in enumerate(POOL_WINDOWS):
        cg = csum[..., g * POOL_GROUP:(g + 1) * POOL_GROUP]
        upper = cg[:, 1:]
        lower = jnp.concatenate([jnp.zeros((B, w - 1, POOL_GROUP), jnp.float32),
                                 cg[:, :S - w + 1]], axis=1)
        count = jnp.minimum(t_idx + 1, w).astype(jnp.float32)[None, :, None]
        outs.append((upper - lower) / count)
    pooled = (jnp.concatenate(outs, axis=-1) - x32).astype(x.dtype)
    y = jnp.einsum('bsgc,gcd->bsgd', pooled.reshape(B, S, N_POOL_GROUPS, POOL_GROUP), pool_w)
    return (y.reshape(B, S, D) + pool_b) * pool_scale

def _swiglu(x, w13, w2):
    h = x @ w13
    g, u = jnp.split(h, 2, axis=-1)
    return (jax.nn.silu(g) * u) @ w2

def setup_inputs(seed: int = 0) -> dict:
    key = jax.random.key(seed)
    ks = jax.random.split(key, 24)
    D = D_MODEL
    f32 = jnp.float32
    nrm = lambda k, shape, s: jax.random.normal(k, shape, f32) * s
    return {
        'x': nrm(ks[0], (BATCH, SEQ, D), 1.0),
        'attn_wqkv': nrm(ks[1], (N_ATTN_LAYERS, D, 3 * D), D ** -0.5),
        'attn_wo': nrm(ks[2], (N_ATTN_LAYERS, D, D), BETA * D ** -0.5),
        'attn_lambda': nrm(ks[3], (N_ATTN_LAYERS, 4, HEAD_DIM), LAMBDA_STD),
        'attn_subln_g': 1.0 + nrm(ks[4], (N_ATTN_LAYERS, 2 * HEAD_DIM), 0.02),
        'conv_pw1_w': nrm(ks[5], (N_CONV_LAYERS, D, 2 * D), D ** -0.5),
        'conv_pw1_b': nrm(ks[6], (N_CONV_LAYERS, 2 * D), 0.02),
        'conv_dw_w': nrm(ks[7], (N_CONV_LAYERS, CONV_WIDTH, D), CONV_WIDTH ** -0.5),
        'conv_dw_b': nrm(ks[8], (N_CONV_LAYERS, D), 0.02),
        'conv_ln_g': 1.0 + nrm(ks[9], (N_CONV_LAYERS, D), 0.02),
        'conv_ln_b': nrm(ks[10], (N_CONV_LAYERS, D), 0.02),
        'conv_pw2_w': nrm(ks[11], (N_CONV_LAYERS, D, D), BETA * D ** -0.5),
        'conv_pw2_b': nrm(ks[12], (N_CONV_LAYERS, D), 0.02),
        'pool_w': nrm(ks[13], (N_POOL_LAYERS, N_POOL_GROUPS, POOL_GROUP, POOL_GROUP), BETA * POOL_GROUP ** -0.5),
        'pool_b': nrm(ks[14], (N_POOL_LAYERS, D), 0.02),
        'pool_scale': 1.0 + nrm(ks[15], (N_POOL_LAYERS, D), 0.1),
        'ffn_w13': nrm(ks[16], (DEPTH, D, 2 * D_FF), D ** -0.5),
        'ffn_w2': nrm(ks[17], (DEPTH, D_FF, D), BETA * D_FF ** -0.5),
        'ln1_g': 1.0 + nrm(ks[18], (DEPTH, D), 0.02),
        'ln1_b': nrm(ks[19], (DEPTH, D), 0.02),
        'ln2_g': 1.0 + nrm(ks[20], (DEPTH, D), 0.02),
        'ln2_b': nrm(ks[21], (DEPTH, D), 0.02),
    }

def reference(x, attn_wqkv, attn_wo, attn_lambda, attn_subln_g,
              conv_pw1_w, conv_pw1_b, conv_dw_w, conv_dw_b, conv_ln_g, conv_ln_b,
              conv_pw2_w, conv_pw2_b, pool_w, pool_b, pool_scale,
              ffn_w13, ffn_w2, ln1_g, ln1_b, ln2_g, ln2_b):
    cos, sin = _rope_tables(x.shape[1], x.dtype)
    for i in range(DEPTH):
        mixer, j = i % N_MIXERS, i // N_MIXERS
        if mixer == 0:
            lambda_init = 0.8 - 0.6 * math.exp(-0.3 * i)
            h = _diff_attention(x, attn_wqkv[j], attn_wo[j], attn_lambda[j], attn_subln_g[j],
                                cos, sin, lambda_init)
        elif mixer == 1:
            h = _conformer_conv(x, conv_pw1_w[j], conv_pw1_b[j], conv_dw_w[j], conv_dw_b[j],
                                conv_ln_g[j], conv_ln_b[j], conv_pw2_w[j], conv_pw2_b[j])
        else:
            h = _multiscale_pool(x, pool_w[j], pool_b[j], pool_scale[j])
        x = _layer_norm(ALPHA * x + h, ln1_g[i], ln1_b[i])
        x = _layer_norm(ALPHA * x + _swiglu(x, ffn_w13[i], ffn_w2[i]), ln2_g[i], ln2_b[i])
    return x


_drawn_inputs = setup_inputs


def setup_inputs(seed=0):
    import zlib

    import numpy as np

    out = dict(_drawn_inputs(seed))
    spreads = {}
    factors = {'attn_lambda': 5.94,
     'attn_subln_g': 22.256,
     'conv_pw1_b': 8.0,
     'conv_dw_b': 8.0,
     'conv_ln_g': 24.937,
     'conv_ln_b': 23.495,
     'conv_pw2_b': 4.548,
     'pool_b': 4.57,
     'pool_scale': 3.584}
    for name, (base, spread) in spreads.items():
        noise = np.random.default_rng([zlib.crc32(name.encode()), seed]).standard_normal(out[name].shape)
        drawn = base * np.exp(spread * noise) if base else spread * noise
        out[name] = __import__('jax').numpy.asarray(drawn.astype(out[name].dtype))
    for name, factor in factors.items():
        out[name] = (out[name] * factor).astype(out[name].dtype)
    return out
```

```python
import math
from contextlib import ExitStack

import numpy as np

import concourse.bass as bass
from concourse import mybir

D, SEQ, DEPTH = 1024, 512, 4
P = 128
KD = D // P
TB = SEQ // P
BANK = 512
HEADS, HD = 8, 64
ROT = HD // 4
CONV_W = 31
PAD = CONV_W - 1
WINDOWS = (2, 4, 8, 16)
DFF = int(math.ceil(8 * D / 3 / 256) * 256)
FC = DFF // P
ALPHA = float((2 * DEPTH) ** 0.25)
EPS = 1e-5
RING = 4
LEAD = 2
TAIL = 4
ORDER = (2, 3, 0, 1)
UNIT = 8 * P

MIXER = ("attention", "convolution", "pooling")
UNITS = {"attention": (("v", KD), ("qk", 2 * HEADS), ("wo", KD)),
         "convolution": (("pw1", 2 * KD), ("pw2", KD)),
         "pooling": (("pw", 2),)}


def lambda_init(i):
    return 0.8 - 0.6 * math.exp(-0.3 * i)


def first_units():
    at, n = {}, 0
    for i in range(DEPTH):
        for stage, count in UNITS[MIXER[i % 3]] + (("up", 2 * FC), ("down", FC)):
            at[i, stage] = n
            n += count
    return at, n


def column_layout():
    at, n = {}, 0
    for j in range((DEPTH + 2) // 3):
        at["subln_g", j] = n
        n += 1
    for j in range((DEPTH + 1) // 3):
        for name, count in (("pw1_b", 2 * KD), ("dw_b", KD), ("cln_g", KD), ("cln_b", KD), ("dw_w", CONV_W * KD)):
            at[name, j] = n
            n += count
    return at, n


C_IDENT, C_MASK, C_SWAP, C_COS, C_SIN = 0, P, 2 * P, 3 * P, 3 * P + SEQ
C_COUNT = C_SIN + SEQ
CMAX = max(WINDOWS)
C_ONES = C_COUNT + len(WINDOWS) * CMAX
C_ALL = C_ONES + P


def build(nc, x, wqkv, wo, lam, pw1, pw2, pw2_b, pool_w, pool_b, pool_s, w13, w2, g1, b1, g2, b2,
          columns, constants, out):
    f32, f32r, bf16 = mybir.dt.float32, mybir.dt.float32r, mybir.dt.bfloat16
    ALU, ACT, AX = mybir.AluOpType, mybir.ActivationFunctionType, mybir.AxisListType
    unit0, n_units = first_units()
    col, n_cols = column_layout()
    ctx = ExitStack()

    def sb(name, shape, dt=f32):
        return ctx.enter_context(nc.sbuf_tensor(name, shape, dt))

    def sem(name):
        return ctx.enter_context(nc.semaphore(name))

    x_nat = sb("x_nat", [P, TB, D])
    xT_hi = sb("xT_hi", [P, KD, SEQ], f32r)
    xT_lo = sb("xT_lo", [P, KD, SEQ], f32r)
    hid = sb("hid", [P, FC * SEQ])
    raw = sb("raw", [P, RING, UNIT])
    w_hi = sb("w_hi", [P, RING, UNIT], f32r)
    w_lo = sb("w_lo", [P, RING, UNIT], f32r)
    a_hi = sb("a_hi", [P, RING, SEQ], f32r)
    a_lo = sb("a_lo", [P, RING, SEQ], f32r)
    gate = sb("gate", [P, 2, SEQ])
    ln_gb = sb("ln_gb", [P, 2, D])
    mix_gb = sb("mix_gb", [P, 2, D])
    cols = sb("cols", [P, n_cols])
    cst = sb("cst", [P, C_ALL])
    ident = cst[:, C_IDENT:C_IDENT + P]
    ident_b = sb("ident_b", [P, P], bf16)
    mask_b = sb("mask_b", [P, P], bf16)
    swap_r = sb("swap_r", [P, P], f32r)
    lam_all = sb("lam_all", [P, 2, 4 * HD])
    lam_s = sb("lam_s", [P, 2, 2])
    neg_lam = sb("neg_lam", [P, 2])
    gain = sb("gain", [P, 2])
    stats = sb("stats", [P, 2, 2, 6])
    mean_var = sb("mean_var", [P, 2, 2])
    var_eps = sb("var_eps", [P, 2])
    rstd = sb("rstd", [P, 2])
    neg_half = sb("neg_half", [P, TB])
    prob = sb("prob", [P, 2, 2, SEQ])
    diff = sb("diff", [P, 2, SEQ])
    diffT = sb("diffT", [P, 2, SEQ])
    neg_max = sb("neg_max", [P, 2, 2])
    den = sb("den", [P, 2, 2])
    rden = sb("rden", [P, 2, 2])
    rden0 = sb("rden0", [P, 2, TB])
    coef = sb("coef", [P, 2])
    o_nat = sb("o_nat", [P, TB, P])
    o_ms = sb("o_ms", [P, TB])
    o_rstd = sb("o_rstd", [P, TB])

    v_nat = hid[:, 0:TB * D].rearrange("p (t n) -> p t n", t=TB)
    oT0 = TB * D
    qk0 = oT0 + KD * SEQ
    qkT = hid[:, qk0:qk0 + 4 * SEQ].rearrange("p (r s n) -> p r s n", r=2, s=2)
    glu = hid[:, 0:KD * (PAD + SEQ)]
    dw0 = KD * (PAD + SEQ)
    xT0, pool0 = 0, KD * SEQ

    ps = ctx.enter_context(nc.psum_tensor("ps", [P, 8, BANK], f32))
    O_BANK, S_BANK, T_BANK = 2, 3, 7

    raw_loaded = [sem(f"raw_loaded{r}") for r in range(RING)]
    x_loaded, col_loaded, cst_loaded, lam_loaded = sem("x_loaded"), sem("col_loaded"), sem("cst_loaded"), sem("lam_loaded")
    ln_loaded, mix_loaded, stored = sem("ln_loaded"), sem("mix_loaded"), sem("stored")
    w_hi_done, w_lo_done, w_used = sem("w_hi_done"), sem("w_lo_done"), sem("w_used")
    a_hi_done, a_lo_done = sem("a_hi_done"), sem("a_lo_done")
    gate_done, gated = sem("gate_done"), sem("gated")
    y_ready, var_ready, rstd_ready, x_new = sem("y_ready"), sem("var_ready"), sem("rstd_ready"), sem("x_new")
    xT_ready, xT_hi_done, xT_lo_done, xT_kept = sem("xT_ready"), sem("xT_hi_done"), sem("xT_lo_done"), sem("xT_kept")
    resid_ready, pool_step = sem("resid_ready"), sem("pool_step")
    setup_act, setup_dve, setup_pool, lam_prod, lam_exp = (sem("setup_act"), sem("setup_dve"), sem("setup_pool"),
                                                           sem("lam_prod"), sem("lam_exp"))
    v_done = sem("v_done")
    rope_hi, rope_lo, swapped, roped = sem("rope_hi"), sem("rope_lo"), sem("swapped"), sem("roped")
    s_ready, max_done, exp_done, diff_done = sem("s_ready"), sem("max_done"), sem("exp_done"), sem("diff_done")
    diff_turned, diffT_done, pv_done = sem("diff_turned"), sem("diffT_done"), sem("pv_done")
    o_scaled, o_squared, o_ms_done, o_rstd_done, o_normed, o_turned, oT_done = (
        sem("o_scaled"), sem("o_squared"), sem("o_ms_done"), sem("o_rstd_done"), sem("o_normed"),
        sem("o_turned"), sem("oT_done"))
    pool_used = sem("pool_used")
    mix_scratch = mix_gb[:, :, 0:SEQ]
    conv_done, mean_done, centred, squared, cvar_done, cstd_done, cnormed, act_done = (
        sem("conv_done"), sem("mean_done"), sem("centred"), sem("squared"), sem("cvar_done"),
        sem("cstd_done"), sem("cnormed"), sem("act_done"))
    pooled = sem("pooled")
    dve_step = sem("dve_step")

    def gated_before(i, stage):
        n = 0
        for j in range(i):
            n += FC + (KD if MIXER[j % 3] == "convolution" else 0)
        return n + (KD if stage == "up" and MIXER[i % 3] == "convolution" else 0)

    def chunks_before(i, stage):
        n = 0
        for j in range(i + 1):
            if j == i and stage != "down":
                return n
            n += KD
            if j < i:
                n += FC
        return n

    def loaded(u):
        return 16 * (u // RING + 1)

    DOWN = {"attention": "wo", "convolution": "pw2", "pooling": "pw"}

    block = ctx.enter_context(nc.Block())

    @block.sync
    def _(sp):
        def load(u, src, i=None):
            r = u % RING
            step = 0 if i is None else i * RING
            if u >= RING:
                sp.wait_ge(w_hi_done, step + (u - RING + 1))
                sp.wait_ge(w_lo_done, step + (u - RING + 1))
            sp.dma_start(raw[:, r, :] if len(src.shape) == 2 else raw[:, r, :].rearrange("p (k n) -> p k n", n=src.shape[2]),
                         src).then_inc(raw_loaded[r], 16)

        def by_rows(w, c):
            return w[bass.ds(c * P, P), 0:D] if not isinstance(c, int) else w[c * P:(c + 1) * P, 0:D]

        def by_columns(w, c):
            v = w.rearrange("(k p) n -> p k n", p=P)
            return v[:, :, bass.ds(c, P)]

        def load_rows(w, u0, n):
            k = n % RING
            for c in range(k):
                load(u0 + c, by_rows(w, c))
            if n >= RING:
                with sp.Fori(0, n // RING) as i:
                    for c in range(RING):
                        load(u0 + k + c, by_rows(w, i * RING + (k + c)), i)

        def load_pairs(w, u0, n, first, second):
            for c in range(2):
                load(u0 + 2 * c, by_columns(w, first + c * P))
                load(u0 + 2 * c + 1, by_columns(w, second + c * P))
            with sp.Fori(0, n // 2 - 1) as i:
                for c in range(2):
                    for s, start in enumerate((first, second)):
                        load(u0 + RING + 2 * c + s, by_columns(w, i * (2 * P) + (start + (2 + c) * P)), i)

        for t in ORDER:
            sp.dma_start(x_nat[:, t, :], x[t * P:(t + 1) * P, :]).then_inc(x_loaded, 16)
        sp.dma_start(cst[:, :], constants).then_inc(cst_loaded, 16)
        for i in range(DEPTH):
            j = i // 3
            mixer = MIXER[i % 3]
            if mixer == "attention":
                for c in range(KD):
                    load(unit0[i, "v"] + c, wqkv[j, c * P:(c + 1) * P, 2 * D:3 * D])
                load_pairs(wqkv[j], unit0[i, "qk"], HEADS, 0, D)
                load_rows(wo[j], unit0[i, "wo"], KD)
            elif mixer == "convolution":
                load_pairs(pw1[j], unit0[i, "pw1"], KD, 0, D)
                load_rows(pw2[j], unit0[i, "pw2"], KD)
            else:
                for c in range(2):
                    load(unit0[i, "pw"] + c, pool_w[j, :, c * P:(c + 1) * P, :].rearrange("g p n -> p g n"))
            load_pairs(w13[i], unit0[i, "up"], FC, 0, DFF)
            load_rows(w2[i], unit0[i, "down"], FC)
        for s, t in enumerate(ORDER):
            sp.wait_ge(x_new, TB * (2 * DEPTH - 1) + s + 1)
            sp.dma_start(out[t * P:(t + 1) * P, :], x_nat[:, t, :]).then_inc(stored, 16)
        sp.wait_ge(stored, 16 * TB)

    @block.gpsimd
    def _(pool):
        nc.gpsimd.memset(neg_half[:, :], -0.5).then_inc(setup_pool, 1)
        pool.dma_start(cols[:, :], columns).then_inc(col_loaded, 16)
        for j in range(2):
            pool.dma_start(lam_all[:, j, :], lam[j:j + 1, :].to_broadcast([P, 4 * HD])).then_inc(lam_loaded, 16)
        pool.wait_ge(setup_pool, 1)
        steps = 0
        heads = 0
        for i in range(DEPTH):
            mixer = MIXER[i % 3]
            for half, (g, b) in enumerate(((g1, b1), (g2, b2))):
                n = 2 * i + half
                if n:
                    pool.wait_ge(x_new, TB * n)
                pool.dma_start(ln_gb[:, 0, :], g[i:i + 1, :].to_broadcast([P, D])).then_inc(ln_loaded, 16)
                pool.dma_start(ln_gb[:, 1, :], b[i:i + 1, :].to_broadcast([P, D])).then_inc(ln_loaded, 16)
                if half == 0 and mixer == "attention":
                    with pool.Fori(0, HEADS) as h:
                        pool.wait_ge(o_ms_done, h + (heads + 1))
                        nc.gpsimd.tensor_tensor(o_rstd[:, :], o_ms[:, :], neg_half[:, :], ALU.pow).then_inc(o_rstd_done, 1)
                    heads += HEADS
                if half == 0 and mixer != "attention":
                    if mixer == "convolution":
                        pool.dma_start(mix_gb[:, 1, :], pw2_b[i // 3:i // 3 + 1, :].to_broadcast([P, D])).then_inc(mix_loaded, 16)
                        pool.wait_ge(mix_loaded, 16)
                    else:
                        pool.wait_ge(x_new, TB * n)
                        pool.dma_start(mix_gb[:, 0, :], pool_s[i // 3:i // 3 + 1, :].to_broadcast([P, D])).then_inc(mix_loaded, 16)
                        pool.dma_start(mix_gb[:, 1, :], pool_b[i // 3:i // 3 + 1, :].to_broadcast([P, D])).then_inc(mix_loaded, 16)
                        pool.wait_ge(mix_loaded, 48)
                        nc.gpsimd.tensor_tensor(mix_gb[:, 1, :], mix_gb[:, 1, :], mix_gb[:, 0, :], ALU.mult).then_inc(pool_step, 1)
                        steps += 1
                        pool.wait_ge(pool_step, steps)
                    pool.wait_ge(xT_ready, TB * (n + 1))
                    for t in ORDER:
                        nc.gpsimd.tensor_scalar(x_nat[:, t, :], x_nat[:, t, :], ALPHA, 1.0, ALU.mult, ALU.mult).then_inc(pool_step, 1)
                        steps += 1
                        pool.wait_ge(pool_step, steps)
                        nc.gpsimd.tensor_tensor(x_nat[:, t, :], x_nat[:, t, :], mix_gb[:, 1, :], ALU.add).then_inc(resid_ready, 1)
                for s in range(TB):
                    pool.wait_ge(var_ready, TB * n + s + 1)
                    nc.gpsimd.tensor_tensor(rstd[:, s % 2:s % 2 + 1], var_eps[:, s % 2:s % 2 + 1],
                                            neg_half[:, 0:1], ALU.pow).then_inc(rstd_ready, 1)

    @block.scalar
    def _(act):
        def split_w(u, i=None, scale=RING):
            r = u % RING
            step = 0 if i is None else i * scale
            turns = 0 if i is None else i * (16 * (scale // RING))
            act.wait_ge(raw_loaded[r], turns + loaded(u))
            if u >= RING:
                act.wait_ge(w_used, step + (u - RING + 1))
            nc.scalar.activation(w_hi[:, r, :], raw[:, r, :], ACT.Copy).then_inc(w_hi_done, 1)

        def split_a(src, slot):
            nc.scalar.activation(a_hi[:, slot, :], src, ACT.Copy).then_inc(a_hi_done, 1)

        def transposed(b, s, keep=False):
            t = ORDER[s]
            act.wait_ge(xT_ready, TB * b + s + 1)
            src = ps[:, 2 * t:2 * t + 2, :].rearrange("p b (k n) -> p (b k) n", n=P)
            if keep:
                kept = hid[:, xT0:xT0 + KD * SEQ].rearrange("p (k n) -> p k n", n=SEQ)
                nc.scalar.activation(kept[:, :, t * P:(t + 1) * P], src, ACT.Copy).then_inc(xT_kept, 1)
            nc.scalar.activation(xT_hi[:, :, t * P:(t + 1) * P], src, ACT.Copy).then_inc(xT_hi_done, 1)

        def up(i, stage, n, func, bias):
            u0, g0 = unit0[i, stage], gated_before(i, stage)
            which = 0 if stage == "up" else 1
            last_done = (lambda: None)

            def pair(c, it=None, ahead=True):
                if ahead:
                    for k in range(2):
                        split_w(u0 + 2 * c + LEAD + k, it)
                step = 0 if it is None else it * RING
                act.wait_ge(w_used, step + (u0 + 2 * c + which + 1))
                if g0 + c >= 2:
                    act.wait_ge(gated, (0 if it is None else it * 2) + (g0 + c - 1))
                kind = dict(bias=bias(c)) if bias else {}
                nc.scalar.activation(gate[:, c % 2, :], ps[:, 2 * (c % 2) + which, :], func, **kind).then_inc(gate_done, 1)

            if bias is None:
                for c in range(2):
                    pair(c)
                with act.Fori(0, n // 2 - 2) as it:
                    for c in range(2, 4):
                        pair(c, it)
                pair(n - 2)
                pair(n - 1)
            else:
                for c in range(n):
                    pair(c)

        def down(i, stage, n, base, arrived):
            u0 = unit0[i, stage]

            def chunk(c, it=None):
                arrived(c, it)
                if c >= RING:
                    act.wait_ge(w_used, (0 if it is None else it * RING) + (u0 + c - RING + 1))
                src = hid[:, base + c * SEQ:base + (c + 1) * SEQ] if it is None else \
                    hid[:, bass.ds(it * (RING * SEQ) + (base + c * SEQ), SEQ)]
                split_a(src, c % RING)

            chunk(0)
            chunk(1)
            body = n - TAIL - LEAD
            for c in range(body % RING):
                split_w(u0 + c + LEAD)
                chunk(c + LEAD)
            k = body % RING
            if body >= RING:
                with act.Fori(0, body // RING) as it:
                    for c in range(k, k + RING):
                        split_w(u0 + c + LEAD, it)
                        chunk(c + LEAD, it)
            for c in range(body, body + TAIL):
                split_w(u0 + c + LEAD)
                chunk(c + LEAD)

        def blocks(i, half, keep=False):
            b = 2 * i + half + 1
            if b == 2 * DEPTH:
                return
            for s in range(TB):
                if s == TB - 1:
                    nxt = unit0[i, "up"] if half == 0 else unit0[i + 1, UNITS[MIXER[(i + 1) % 3]][0][0]]
                    for k in range(LEAD):
                        split_w(nxt + k)
                transposed(b, s, keep)

        act.wait_ge(cst_loaded, 16)
        nc.scalar.activation(ident_b[:, :], ident, ACT.Copy).then_inc(setup_act, 1)
        nc.scalar.activation(mask_b[:, :], cst[:, C_MASK:C_MASK + P], ACT.Copy).then_inc(setup_act, 1)
        nc.scalar.activation(swap_r[:, :], cst[:, C_SWAP:C_SWAP + P], ACT.Copy).then_inc(setup_act, 1)
        for s in range(TB):
            transposed(0, s)
        for k in range(LEAD):
            split_w(k)
        act.wait_ge(lam_prod, 1)
        nc.scalar.activation(lam_s[:, :, :], lam_s[:, :, :], ACT.Exp).then_inc(lam_exp, 1)

        heads = 0
        for i in range(DEPTH):
            mixer = MIXER[i % 3]
            if mixer == "attention":
                for c in range(KD):
                    split_w(unit0[i, "v"] + c + LEAD)
                for s, t in enumerate(ORDER):
                    act.wait_ge(w_used, unit0[i, "v"] + KD)
                    nc.scalar.activation(v_nat[:, t, :].rearrange("p (b n) -> p b n", b=2), ps[:, 2 * t:2 * t + 2, :],
                                         ACT.Copy).then_inc(v_done, 1)
                u0, H0 = unit0[i, "qk"], heads

                def rope_part(r, it=None):
                    act.wait_ge(w_used, (0 if it is None else it * RING) + (u0 + r + 1))
                    nc.scalar.activation(a_hi[:, r % 2, :], ps[:, r % 2, :], ACT.Copy,
                                         scale=HD ** -0.5 if r % 2 == 0 else 1.0).then_inc(rope_hi, 1)

                def at(it, n, base):
                    return base if it is None else it * (2 * n) + base

                def exps(j, c, it):
                    k = TB * (H0 + j) + c
                    act.wait_ge(max_done, at(it, TB, k + 1))
                    w = (c + 1) * P
                    for m in range(2):
                        e = nc.scalar.activation(prob[:, c % 2, m, 0:w], ps[:, S_BANK + 2 * (c % 2) + m, 0:w], ACT.Exp,
                                                 bias=neg_max[:, c % 2, m:m + 1], accum_out=den[:, c % 2, m:m + 1])
                    e.then_inc(exp_done, 1)

                def turned(j, c, it):
                    act.wait_ge(diff_turned, at(it, TB, TB * (H0 + j) + c + 1))
                    w = (c + 1) * P
                    nc.scalar.activation(diffT[:, c % 2, 0:w], ps[:, T_BANK, 0:w], ACT.Copy).then_inc(diffT_done, 1)

                def square(j, it):
                    act.wait_ge(o_scaled, at(it, 1, H0 + j + 1))
                    nc.scalar.activation(gate[:, 0, :], o_nat[:, :, :], ACT.Square).then_inc(o_squared, 1)

                def out_head(j, it):
                    act.wait_ge(o_turned, at(it, 1, H0 + j + 1))
                    lo = oT0 + j * SEQ
                    dst = hid[:, lo:lo + SEQ] if it is None else hid[:, bass.ds(it * (2 * SEQ) + lo, SEQ)]
                    nc.scalar.activation(dst, ps[:, O_BANK, :], ACT.Copy, scale=gain[:, i // 3:i // 3 + 1]).then_inc(oT_done, 1)

                def step(j, it=None):
                    k_next, q_next, prev = j + 1 < HEADS, j + 2 < HEADS, j > 0
                    exps(j, 0, it)
                    if k_next:
                        split_w(u0 + 2 * j + 3 + LEAD, it)
                    exps(j, 1, it)
                    if prev:
                        square(j - 1, it)
                    if k_next:
                        rope_part(2 * j + 3, it)
                    if prev:
                        out_head(j - 1, it)
                    turned(j, 0, it)
                    exps(j, 2, it)
                    if q_next:
                        split_w(u0 + 2 * j + 4 + LEAD, it)
                    turned(j, 1, it)
                    exps(j, 3, it)
                    turned(j, 2, it)
                    if q_next:
                        rope_part(2 * j + 4, it)
                    turned(j, 3, it)

                for r in range(3):
                    split_w(u0 + r + LEAD)
                    rope_part(r)
                step(0)
                step(1)
                with act.Fori(0, HEADS // 2 - 2) as it:
                    step(2, it)
                    step(3, it)
                step(HEADS - 2)
                step(HEADS - 1)
                square(HEADS - 1, None)
                out_head(HEADS - 1, None)
                heads += HEADS
                def arrived(c, it):
                    act.wait_ge(oT_done, H0 + HEADS)
                down(i, "wo", KD, oT0, arrived)
                blocks(i, 0)
            elif mixer == "convolution":
                c0 = col["pw1_b", i // 3] + KD
                up(i, "pw1", KD, ACT.Sigmoid, lambda c: cols[:, c0 + c:c0 + c + 1])
                for c in range(KD):
                    act.wait_ge(centred, c + 1)
                    if c >= 2:
                        act.wait_ge(squared, c - 1)
                    nc.scalar.activation(gate[:, c % 2, :], hid[:, dw0 + c * SEQ:dw0 + (c + 1) * SEQ], ACT.Square).then_inc(act_done, 1)
                act.wait_ge(cvar_done, 1)
                nc.scalar.activation(gate[:, 0, :], gate[:, 0, :], ACT.Sqrt).then_inc(cstd_done, 1)
                for c in range(KD):
                    act.wait_ge(cnormed, c + 1)
                    src = hid[:, dw0 + c * SEQ:dw0 + (c + 1) * SEQ]
                    cg, cb = col["cln_g", i // 3] + c, col["cln_b", i // 3] + c
                    nc.scalar.activation(src, src, ACT.Silu, bias=cols[:, cb:cb + 1], scale=cols[:, cg:cg + 1]).then_inc(act_done, 1)

                def arrived(c, it):
                    act.wait_ge(act_done, KD + c + 1)
                down(i, "pw2", KD, dw0, arrived)
                blocks(i, 0)
            else:
                for c in range(KD):
                    act.wait_ge(pooled, c + 1)
                    if c >= RING:
                        act.wait_ge(xT_kept, TB)
                        act.wait_ge(pool_used, c - RING + 1)
                    split_a(hid[:, pool0 + c * SEQ:pool0 + (c + 1) * SEQ], c % RING)
                blocks(i, 0)
            up(i, "up", FC, ACT.Silu, None)
            g0 = gated_before(i, "up")

            def arrived(c, it):
                act.wait_ge(gated, (0 if it is None else it * RING) + (g0 + c + 1))
            down(i, "down", FC, 0, arrived)
            blocks(i, 1, keep=i + 1 < DEPTH and MIXER[(i + 1) % 3] == "pooling")

    @block.vector
    def _(dve):
        steps = [0]

        def link(ins, it=None, per=0):
            steps[0] += 1
            ins.then_inc(dve_step, 1)
            dve.wait_ge(dve_step, steps[0] if it is None else it * per + steps[0])

        def split_w(u, it=None):
            r = u % RING
            dve.wait_ge(w_hi_done, (0 if it is None else it * RING) + (u + 1))
            nc.vector.tensor_tensor(w_lo[:, r, :], raw[:, r, :], w_hi[:, r, :].bitcast(f32), ALU.subtract).then_inc(w_lo_done, 1)

        def split_a(src, slot, n):
            dve.wait_ge(a_hi_done, n)
            nc.vector.tensor_tensor(a_lo[:, slot, :], src, a_hi[:, slot, :].bitcast(f32), ALU.subtract).then_inc(a_lo_done, 1)

        def down(i, stage, n, base):
            u0, a0 = unit0[i, stage], chunks_before(i, stage)

            def chunk(c, it=None):
                src = hid[:, base + c * SEQ:base + (c + 1) * SEQ] if it is None else \
                    hid[:, bass.ds(it * (RING * SEQ) + (base + c * SEQ), SEQ)]
                split_a(src, c % RING, (0 if it is None else it * RING) + (a0 + c + 1))

            chunk(0)
            chunk(1)
            body = n - TAIL - LEAD
            k = body % RING
            for c in range(k):
                split_w(u0 + c + LEAD)
                chunk(c + LEAD)
            if body >= RING:
                with dve.Fori(0, body // RING) as it:
                    for c in range(k, k + RING):
                        split_w(u0 + c + LEAD, it)
                        chunk(c + LEAD, it)
            for c in range(body, body + TAIL):
                split_w(u0 + c + LEAD)
                chunk(c + LEAD)

        def normalise(i, half, s, last_unit):
            n, t = 2 * i + half, ORDER[s]
            mixer = MIXER[i % 3] if half == 0 else None
            if s < TB - 1:
                dve.wait_ge(y_ready, (TB - 1) * n + s + 1)
            else:
                dve.wait_ge(w_used, last_unit + 1)
            xs, y = x_nat[:, t, :], ps[:, 2 * t:2 * t + 2, :].rearrange("p b n -> p (b n)")
            if mixer == "convolution":
                dve.wait_ge(resid_ready, s + 1)
                link(nc.vector.tensor_tensor(xs, xs, y, ALU.add))
            elif mixer == "pooling":
                dve.wait_ge(resid_ready, TB + s + 1)
                scaled = gate[:, :, :].rearrange("p b n -> p (b n)")
                link(nc.vector.tensor_tensor(scaled, y, mix_gb[:, 0, :], ALU.mult))
                link(nc.vector.tensor_tensor(xs, xs, scaled, ALU.add))
            else:
                link(nc.vector.scalar_tensor_tensor(xs, xs, ALPHA, y, ALU.mult, ALU.add))
            for h in range(2):
                st = nc.vector.bn_stats(stats[:, s % 2, h, :], x_nat[:, t, h * BANK:(h + 1) * BANK])
            link(st)
            link(nc.vector.bn_aggr(mean_var[:, s % 2, :], stats[:, s % 2, :, :].rearrange("p h n -> p (h n)")))
            nc.vector.tensor_scalar(var_eps[:, s % 2:s % 2 + 1], mean_var[:, s % 2, 1:2], EPS, None, ALU.add).then_inc(var_ready, 1)
            if s == 0:
                dve.wait_ge(ln_loaded, 32 * (n + 1))
            link(nc.vector.scalar_tensor_tensor(xs, xs, mean_var[:, s % 2, 0:1], ln_gb[:, 0, :], ALU.subtract, ALU.mult))
            dve.wait_ge(rstd_ready, TB * n + s + 1)
            nc.vector.scalar_tensor_tensor(xs, xs, rstd[:, s % 2:s % 2 + 1], ln_gb[:, 1, :], ALU.mult, ALU.add).then_inc(x_new, 1)

        def transposed(b, s):
            t = ORDER[s]
            dve.wait_ge(xT_hi_done, TB * b + s + 1)
            src = ps[:, 2 * t:2 * t + 2, :].rearrange("p b (k n) -> p (b k) n", n=P)
            at = slice(t * P, (t + 1) * P)
            nc.vector.tensor_tensor(xT_lo[:, :, at], src, xT_hi[:, :, at].bitcast(f32), ALU.subtract).then_inc(xT_lo_done, 1)

        def blocks(i, half, last_unit):
            b = 2 * i + half + 1
            for s in range(TB):
                normalise(i, half, s, last_unit)
                if s and b < 2 * DEPTH:
                    transposed(b, s - 1)
            if b < 2 * DEPTH:
                nxt = unit0[i, "up"] if half == 0 else unit0[i + 1, UNITS[MIXER[(i + 1) % 3]][0][0]]
                for k in range(LEAD):
                    split_w(nxt + k)
                transposed(b, TB - 1)

        dve.wait_ge(lam_loaded, 32)
        l4 = lam_all[:, :, :].rearrange("p j (m s d) -> p j m s d", m=2, s=2)
        prod = gate[:, 0, 0:4 * HD].rearrange("p (j m d) -> p j m d", j=2, m=2)
        link(nc.vector.tensor_tensor(prod, l4[:, :, :, 0, :], l4[:, :, :, 1, :], ALU.mult))
        nc.vector.tensor_reduce(lam_s[:, :, :], prod, AX.X, ALU.add).then_inc(lam_prod, 1)
        for s in range(TB):
            transposed(0, s)
        for k in range(LEAD):
            split_w(k)
        dve.wait_ge(lam_exp, 1)
        link(nc.vector.tensor_tensor(neg_lam[:, :], lam_s[:, :, 1], lam_s[:, :, 0], ALU.subtract))
        dve.wait_ge(col_loaded, 16)
        for j in range(2):
            c = col["subln_g", j]
            nc.vector.tensor_scalar(neg_lam[:, j:j + 1], neg_lam[:, j:j + 1], lambda_init(3 * j), None, ALU.subtract)
            g = nc.vector.tensor_scalar(gain[:, j:j + 1], cols[:, c:c + 1], 1.0 - lambda_init(3 * j), None, ALU.mult)
        link(g)

        heads = 0
        for i in range(DEPTH):
            mixer = MIXER[i % 3]
            if mixer == "attention":
                for c in range(KD):
                    split_w(unit0[i, "v"] + c + LEAD)
                u0, H0, j3 = unit0[i, "qk"], heads, i // 3
                PER = 2 * (4 * 2 + 1 + 2)

                def at(it, n, base):
                    return base if it is None else it * (2 * n) + base

                def head_max(j, c, it):
                    k = TB * (H0 + j) + c
                    dve.wait_ge(s_ready, at(it, TB, k + 1))
                    src = ps[:, S_BANK + 2 * (c % 2):S_BANK + 2 * (c % 2) + 2, 0:(c + 1) * P]
                    nc.vector.tensor_reduce(neg_max[:, c % 2, :], src, AX.X, ALU.max, negate=True).then_inc(max_done, 1)

                def combine(j, c, it):
                    dve.wait_ge(exp_done, at(it, TB, TB * (H0 + j) + c + 1))
                    par, w = c % 2, (c + 1) * P
                    nc.vector.reciprocal(rden0[:, j % 2, c:c + 1], den[:, par, 0:1])
                    link(nc.vector.reciprocal(rden[:, par, 1:2], den[:, par, 1:2]), it, PER)
                    link(nc.vector.scalar_tensor_tensor(coef[:, par:par + 1], den[:, par, 0:1], rden[:, par, 1:2],
                                                        neg_lam[:, j3:j3 + 1], ALU.mult, ALU.mult), it, PER)
                    nc.vector.scalar_tensor_tensor(diff[:, par, 0:w], prob[:, par, 1, 0:w], coef[:, par:par + 1],
                                                   prob[:, par, 0, 0:w], ALU.mult, ALU.add).then_inc(diff_done, 1)

                def scale_head(j, it):
                    dve.wait_ge(pv_done, at(it, TB, TB * (H0 + j + 1)))
                    nc.vector.tensor_tensor(o_nat[:, :, :], ps[:, O_BANK, :].rearrange("p (t n) -> p t n", t=TB),
                                            rden0[:, j % 2, :].unsqueeze(2).to_broadcast([P, TB, P]), ALU.mult).then_inc(o_scaled, 1)

                def mean_square(j, it):
                    dve.wait_ge(o_squared, at(it, 1, H0 + j + 1))
                    link(nc.vector.tensor_reduce(o_ms[:, :], gate[:, 0, :].rearrange("p (t n) -> p t n", t=TB), AX.X, ALU.add), it, PER)
                    nc.vector.tensor_scalar(o_ms[:, :], o_ms[:, :], 1.0 / (2 * HD), EPS, ALU.mult, ALU.add).then_inc(o_ms_done, 1)

                def norm_head(j, it):
                    dve.wait_ge(o_rstd_done, at(it, 1, H0 + j + 1))
                    nc.vector.tensor_tensor(o_nat[:, :, :], o_nat[:, :, :], o_rstd[:, :].unsqueeze(2).to_broadcast([P, TB, P]),
                                            ALU.mult).then_inc(o_normed, 1)

                def rope_first(r, it=None):
                    s, scale = r % 2, HD ** -0.5 if r % 2 == 0 else 1.0
                    dve.wait_ge(rope_hi, at(it, 2, 2 * H0 + r + 1))
                    nc.vector.scalar_tensor_tensor(mix_scratch[:, s, :], ps[:, s, :], scale, cst[:, C_COS:C_COS + SEQ], ALU.mult, ALU.mult)
                    nc.vector.scalar_tensor_tensor(a_lo[:, s, :], ps[:, s, :], scale, a_hi[:, s, :].bitcast(f32),
                                                   ALU.mult, ALU.subtract).then_inc(rope_lo, 1)

                def rope_second(r, it=None):
                    s, par = r % 2, r // 2 % 2
                    dve.wait_ge(swapped, at(it, 2, 2 * H0 + r + 1))
                    link(nc.vector.tensor_tensor(qkT[:, par, s, :], ps[:, s, :], cst[:, C_SIN:C_SIN + SEQ], ALU.mult), it, PER)
                    nc.vector.tensor_tensor(qkT[:, par, s, :], qkT[:, par, s, :], mix_scratch[:, s, :], ALU.add).then_inc(roped, 1)

                def step(j, it=None):
                    k_next, q_next, prev = j + 1 < HEADS, j + 2 < HEADS, j > 0
                    head_max(j, 0, it)
                    if prev:
                        scale_head(j - 1, it)
                    head_max(j, 1, it)
                    combine(j, 0, it)
                    if prev:
                        mean_square(j - 1, it)
                    if k_next:
                        split_w(u0 + 2 * j + 3 + LEAD, it)
                    if prev:
                        norm_head(j - 1, it)
                    combine(j, 1, it)
                    if k_next:
                        rope_first(2 * j + 3, it)
                    head_max(j, 2, it)
                    combine(j, 2, it)
                    if k_next:
                        rope_second(2 * j + 3, it)
                    if q_next:
                        split_w(u0 + 2 * j + 4 + LEAD, it)
                    head_max(j, 3, it)
                    combine(j, 3, it)
                    if q_next:
                        rope_first(2 * j + 4, it)
                        rope_second(2 * j + 4, it)

                for r in range(3):
                    split_w(u0 + r + LEAD)
                    rope_first(r)
                    rope_second(r)
                step(0)
                step(1)
                before = steps[0]
                with dve.Fori(0, HEADS // 2 - 2) as it:
                    step(2, it)
                    step(3, it)
                assert steps[0] - before == PER
                steps[0] = before + PER * (HEADS // 2 - 2)
                step(HEADS - 2)
                step(HEADS - 1)
                scale_head(HEADS - 1, None)
                mean_square(HEADS - 1, None)
                norm_head(HEADS - 1, None)
                heads += HEADS
                down(i, "wo", KD, oT0)
                blocks(i, 0, unit0[i, "wo"] + KD - 1)
            elif mixer == "convolution":
                u0, g0 = unit0[i, "pw1"], gated_before(i, "pw1")
                padded = glu.rearrange("p (k n) -> p k n", n=PAD + SEQ)
                link(nc.vector.memset(padded[:, :, 0:PAD], 0.0))
                PER = 2 * PAD

                def taps(c, it):
                    def src(k):
                        at = c * (PAD + SEQ) + k
                        return hid[:, bass.ds(it * (2 * (PAD + SEQ)) + at, SEQ)]

                    def weight(k):
                        at = col["dw_w", 0] + c * CONV_W + k
                        return cols[:, bass.ds(it * (2 * CONV_W) + at, 1)]

                    dst = hid[:, bass.ds(it * (2 * SEQ) + (dw0 + c * SEQ), SEQ)]
                    bias = cols[:, bass.ds(it * 2 + (col["dw_b", 0] + c), 1)]
                    link(nc.vector.tensor_scalar(dst, src(PAD), weight(PAD), bias, ALU.mult, ALU.add), it, PER)
                    for k in range(PAD - 1, 0, -1):
                        link(nc.vector.scalar_tensor_tensor(dst, src(k), weight(k), dst, ALU.mult, ALU.add), it, PER)
                    nc.vector.scalar_tensor_tensor(dst, src(0), weight(0), dst, ALU.mult, ALU.add).then_inc(conv_done, 1)

                before = steps[0]
                with dve.Fori(0, KD // 2) as it:
                    for c in range(2):
                        for k in range(2):
                            split_w(u0 + 2 * c + LEAD + k, it)
                        dve.wait_ge(gate_done, it * 2 + (g0 + c + 1))
                        dve.wait_ge(w_used, it * RING + (u0 + 2 * c + 1))
                        link_at = col["pw1_b", 0] + c
                        nc.vector.scalar_tensor_tensor(hid[:, bass.ds(it * (2 * (PAD + SEQ)) + (c * (PAD + SEQ) + PAD), SEQ)],
                                                       ps[:, 2 * c, :], cols[:, bass.ds(it * 2 + link_at, 1)], gate[:, c, :],
                                                       ALU.add, ALU.mult).then_inc(gated, 1)
                        dve.wait_ge(gated, it * 2 + (g0 + c + 1))
                        taps(c, it)
                assert steps[0] - before == PER
                steps[0] = before + PER * (KD // 2)
                dws = [hid[:, dw0 + c * SEQ:dw0 + (c + 1) * SEQ] for c in range(KD)]
                dve.wait_ge(mean_done, 1)
                for c in range(KD):
                    nc.vector.tensor_tensor(dws[c], dws[c], ps[:, 4, :], ALU.subtract).then_inc(centred, 1)
                dve.wait_ge(squared, KD)
                nc.vector.tensor_scalar(gate[:, 0, :], ps[:, 5, :], EPS, None, ALU.add).then_inc(cvar_done, 1)
                dve.wait_ge(cstd_done, 1)
                link(nc.vector.reciprocal(gate[:, 1, :], gate[:, 0, :]))
                for c in range(KD):
                    nc.vector.tensor_tensor(dws[c], dws[c], gate[:, 1, :], ALU.mult).then_inc(cnormed, 1)
                down(i, "pw2", KD, dw0)
                blocks(i, 0, unit0[i, "pw2"] + KD - 1)
            else:
                a0 = chunks_before(i, "pw")
                dve.wait_ge(xT_kept, TB)
                for c in range(KD):
                    g = c // (KD // len(WINDOWS))
                    w = WINDOWS[g]
                    own = hid[:, xT0 + c * SEQ:xT0 + (c + 1) * SEQ]
                    s = own
                    if c:
                        dve.wait_ge(pooled, c)
                    for m in range(g + 1):
                        sh, d = 1 << m, gate[:, m % 2, :]
                        nc.vector.tensor_copy(d[:, 0:sh], s[:, 0:sh])
                        link(nc.vector.tensor_tensor(d[:, sh:], s[:, sh:], s[:, 0:SEQ - sh], ALU.add))
                        s = d
                    dst = hid[:, pool0 + c * SEQ:pool0 + (c + 1) * SEQ]
                    count = cst[:, C_COUNT + g * CMAX:C_COUNT + (g + 1) * CMAX]
                    link(nc.vector.tensor_tensor(s[:, 0:CMAX], s[:, 0:CMAX], count, ALU.mult))
                    nc.vector.tensor_tensor(dst[:, 0:CMAX], s[:, 0:CMAX], own[:, 0:CMAX], ALU.subtract)
                    nc.vector.scalar_tensor_tensor(dst[:, CMAX:], s[:, CMAX:], 1.0 / w, own[:, CMAX:], ALU.mult, ALU.subtract).then_inc(pooled, 1)
                    if c:
                        b = c - 1
                        split_a(hid[:, pool0 + b * SEQ:pool0 + (b + 1) * SEQ], b % RING, a0 + b + 1)
                b = KD - 1
                split_a(hid[:, pool0 + b * SEQ:pool0 + (b + 1) * SEQ], b % RING, a0 + b + 1)
                blocks(i, 0, unit0[i, "pw"] + 1)
            u0, g0 = unit0[i, "up"], gated_before(i, "up")

            def pair(c, it=None):
                for k in range(2):
                    split_w(u0 + 2 * c + LEAD + k, it)
                dve.wait_ge(gate_done, (0 if it is None else it * 2) + (g0 + c + 1))
                dve.wait_ge(w_used, (0 if it is None else it * RING) + (u0 + 2 * c + 2))
                dst = hid[:, c * SEQ:(c + 1) * SEQ] if it is None else hid[:, bass.ds(it * (2 * SEQ) + c * SEQ, SEQ)]
                nc.vector.tensor_tensor(dst, gate[:, c % 2, :], ps[:, 2 * (c % 2) + 1, :], ALU.mult).then_inc(gated, 1)

            with dve.Fori(0, FC // 2) as it:
                pair(0, it)
                pair(1, it)
            down(i, "down", FC, 0)
            blocks(i, 1, unit0[i, "down"] + FC - 1)

    @block.tensor
    def _(pe):
        def exact(dst, lhs, rhs, start, stop, check=False):
            nc.tensor.matmul(dst, lhs[0], rhs[0], start=start, stop=False, skip_group_check=check)
            nc.tensor.matmul(dst, lhs[0], rhs[1], start=False, stop=False, skip_group_check=check)
            return nc.tensor.matmul(dst, lhs[1], rhs[0], start=False, stop=stop, skip_group_check=check)

        def split_ready(u, it=None):
            step = 0 if it is None else it * RING
            pe.wait_ge(w_hi_done, step + (u + 1))
            pe.wait_ge(w_lo_done, step + (u + 1))

        def up_unit(u, bank, it=None, part=None):
            r = u % RING
            if part != 1:
                split_ready(u, it)
            ks = range(KD) if part is None else range(part * KD // 2, (part + 1) * KD // 2)
            for k in ks:
                w = [x[:, r, k * P:(k + 1) * P] for x in (w_hi, w_lo)]
                m = exact(ps[:, bank, :], w, (xT_hi[:, k, :], xT_lo[:, k, :]), k == 0, k == KD - 1)
            if part != 0:
                m.then_inc(w_used, 1)

        def up(i, stage, n):
            u0, g0 = unit0[i, stage], gated_before(i, stage)

            def pair(c, it=None):
                if g0 + c >= 2:
                    pe.wait_ge(gated, (0 if it is None else it * 2) + (g0 + c - 1))
                for s in range(2):
                    up_unit(u0 + 2 * c + s, 2 * (c % 2) + s, it)

            pair(0)
            pair(1)
            with pe.Fori(0, n // 2 - 1) as it:
                pair(2, it)
                pair(3, it)

        def down_block(acts, u, t, start, stop, half=None):
            r = u % RING
            lhs = [a[:, t * P:(t + 1) * P] for a in acts]
            for h in range(2):
                m = exact(ps[:, 2 * t + h, :], lhs, [w[:, r, h * BANK:(h + 1) * BANK] for w in (w_hi, w_lo)], start, stop)
            return m

        def chunk_ready(n, it=None):
            step = 0 if it is None else it * RING
            pe.wait_ge(a_hi_done, step + n)
            pe.wait_ge(a_lo_done, step + n)

        def turn(b, s):
            t = ORDER[s]
            if b:
                pe.wait_ge(x_new, TB * (b - 1) + s + 1)
            for k in range(KD):
                m = nc.tensor.transpose(ps[:, 2 * t + k // 4, (k % 4) * P:(k % 4 + 1) * P], x_nat[:, t, k * P:(k + 1) * P], ident)
            m.then_inc(xT_ready, 1)

        def turned(b):
            pe.wait_ge(xT_hi_done, TB * (b + 1))
            pe.wait_ge(xT_lo_done, TB * (b + 1))

        def down(i, stage, n, bank_free):
            half = 1 if stage == "down" else 0
            u0, a0, b = unit0[i, stage], chunks_before(i, stage), 2 * i + half + 1

            def acts(c):
                return a_hi[:, c % RING, :], a_lo[:, c % RING, :]

            def chunk(c, it=None):
                chunk_ready(a0 + c + 1, it)
                split_ready(u0 + c, it)
                for s, t in enumerate(ORDER):
                    if c == 0 and s == 2:
                        bank_free()
                    m = down_block(acts(c), u0 + c, t, c == 0, False)
                m.then_inc(w_used, 1)

            body = n - TAIL
            k = body % RING if body % RING else RING
            for c in range(k):
                chunk(c)
            if body > k:
                with pe.Fori(0, (body - k) // RING) as it:
                    for c in range(k, k + RING):
                        chunk(c, it)
            for s, t in enumerate(ORDER):
                for c in range(body, n):
                    if s == 0:
                        chunk_ready(a0 + c + 1)
                        split_ready(u0 + c)
                    m = down_block(acts(c), u0 + c, t, False, c == n - 1)
                    if s == TB - 1:
                        m.then_inc(w_used, 1)
                if s < TB - 1:
                    m.then_inc(y_ready, 1)
                if s and b < 2 * DEPTH:
                    turn(b, s - 1)
            if b < 2 * DEPTH:
                turn(b, TB - 1)
                turned(b)

        pe.wait_ge(cst_loaded, 16)
        pe.wait_ge(x_loaded, 16 * TB)
        for s in range(TB):
            turn(0, s)
        turned(0)
        pe.wait_ge(setup_act, 3)

        heads = 0
        for i in range(DEPTH):
            mixer = MIXER[i % 3]
            if mixer == "attention":
                u0, H0 = unit0[i, "qk"], heads
                for c in range(KD):
                    split_ready(unit0[i, "v"] + c)
                    for t in ORDER:
                        m = down_block((xT_hi[:, c, :], xT_lo[:, c, :]), unit0[i, "v"] + c, t, c == 0, c == KD - 1)
                    m.then_inc(w_used, 1)
                pe.wait_ge(v_done, TB * (i // 3 + 1))

                def at(it, n, base):
                    return base if it is None else it * (2 * n) + base

                def unit(r, it=None, part=None):
                    if r >= 2 and part != 1:
                        pe.wait_ge(roped, at(it, 2, 2 * H0 + r - 1))
                    up_unit(u0 + r, r % 2, it, part)

                def swap(r, it=None):
                    s = r % 2
                    pe.wait_ge(rope_lo, at(it, 2, 2 * H0 + r + 1))
                    nc.tensor.matmul(ps[:, s, :], swap_r[:, :], a_hi[:, s, :], start=True, stop=False)
                    nc.tensor.matmul(ps[:, s, :], swap_r[:, :], a_lo[:, s, :], start=False, stop=True).then_inc(swapped, 1)

                def scores(j, c, it):
                    k = TB * (H0 + j) + c
                    if c == 0:
                        pe.wait_ge(roped, at(it, 2, 2 * (H0 + j + 1)))
                    if k >= 2:
                        pe.wait_ge(exp_done, at(it, TB, k - 1))
                    w = (c + 1) * P
                    for m in range(2):
                        rows = slice(m * HD, (m + 1) * HD)
                        bank = S_BANK + 2 * (c % 2) + m
                        nc.tensor.matmul(ps[:, bank, 0:w], qkT[rows, j % 2, 0, c * P:w], qkT[rows, j % 2, 1, 0:w], start=True, stop=False)
                    for m in range(2):
                        bank = S_BANK + 2 * (c % 2) + m
                        e = nc.tensor.matmul(ps[:, bank, c * P:w], ident_b[:, :], mask_b[:, :], start=False, stop=True)
                    e.then_inc(s_ready, 1)

                def turn_diff(j, c, it):
                    k = TB * (H0 + j) + c
                    pe.wait_ge(diff_done, at(it, TB, k + 1))
                    if k:
                        pe.wait_ge(diffT_done, at(it, TB, k))
                    for kc in range(c + 1):
                        e = nc.tensor.transpose(ps[:, T_BANK, kc * P:(kc + 1) * P], diff[:, c % 2, kc * P:(kc + 1) * P], ident)
                    e.then_inc(diff_turned, 1)

                def values(j, c, it):
                    k = TB * (H0 + j) + c
                    if c == 0 and H0 + j:
                        pe.wait_ge(oT_done, at(it, 1, H0 + j))
                    pe.wait_ge(diffT_done, at(it, TB, k + 1))
                    for kc in range(c + 1):
                        lo = kc * D + j * P
                        v = hid[:, lo:lo + P] if it is None else hid[:, bass.ds(it * (2 * P) + lo, P)]
                        e = nc.tensor.matmul(ps[:, O_BANK, c * P:(c + 1) * P], diffT[:, c % 2, kc * P:(kc + 1) * P], v,
                                             start=kc == 0, stop=kc == c)
                    e.then_inc(pv_done, 1)

                def turn_head(j, it):
                    pe.wait_ge(o_normed, at(it, 1, H0 + j + 1))
                    for c in range(TB):
                        e = nc.tensor.transpose(ps[:, O_BANK, c * P:(c + 1) * P], o_nat[:, c, :], ident)
                    e.then_inc(o_turned, 1)

                def step(j, it=None):
                    k_next, q_next, prev = j + 1 < HEADS, j + 2 < HEADS, j > 0
                    scores(j, 0, it)
                    if k_next:
                        unit(2 * j + 3, it, 0)
                    scores(j, 1, it)
                    if k_next:
                        unit(2 * j + 3, it, 1)
                    if prev:
                        turn_head(j - 1, it)
                    turn_diff(j, 0, it)
                    scores(j, 2, it)
                    values(j, 0, it)
                    if q_next:
                        unit(2 * j + 4, it, 0)
                    if k_next:
                        swap(2 * j + 3, it)
                    turn_diff(j, 1, it)
                    values(j, 1, it)
                    scores(j, 3, it)
                    if q_next:
                        unit(2 * j + 4, it, 1)
                    turn_diff(j, 2, it)
                    values(j, 2, it)
                    turn_diff(j, 3, it)
                    values(j, 3, it)
                    if q_next:
                        swap(2 * j + 4, it)

                for r in range(3):
                    unit(r)
                    swap(r)
                step(0)
                step(1)
                with pe.Fori(0, HEADS // 2 - 2) as it:
                    step(2, it)
                    step(3, it)
                step(HEADS - 2)
                step(HEADS - 1)
                turn_head(HEADS - 1, None)
                heads += HEADS
                down(i, "wo", KD, lambda: pe.wait_ge(oT_done, H0 + HEADS))
            elif mixer == "convolution":
                up(i, "pw1", KD)
                mean = cst[:, C_ONES:C_ONES + P]
                for c in range(KD):
                    pe.wait_ge(conv_done, c + 1)
                    m = nc.tensor.matmul(ps[:, 4, :], mean, hid[:, dw0 + c * SEQ:dw0 + (c + 1) * SEQ], start=c == 0, stop=c == KD - 1)
                m.then_inc(mean_done, 1)
                for c in range(KD):
                    pe.wait_ge(act_done, c + 1)
                    nc.tensor.matmul(ps[:, 5, :], mean, gate[:, c % 2, :], start=c == 0, stop=c == KD - 1).then_inc(squared, 1)
                pe.wait_ge(cvar_done, 1)
                down(i, "pw2", KD, lambda: None)
            else:
                b, u0, a0 = 2 * i + 1, unit0[i, "pw"], chunks_before(i, "pw")
                for k in range(2):
                    split_ready(u0 + k)
                for c in range(KD):
                    g, part = c // 2, c % 2
                    chunk_ready(a0 + c + 1)
                    r, lo = (u0 + part) % RING, g * 2 * P
                    for s, t in enumerate(ORDER):
                        half = (g % 2) * 2 * P
                        m = exact(ps[:, 2 * t + g // 2, half:half + 2 * P], [a[:, c % RING, t * P:(t + 1) * P] for a in (a_hi, a_lo)],
                                  [w[:, r, lo:lo + 2 * P] for w in (w_hi, w_lo)], part == 0, part == 1)
                        if c == KD - 1 and s < TB - 1:
                            m.then_inc(y_ready, 1)
                    if c < RING:
                        m.then_inc(pool_used, 1)
                    elif c >= KD - 2:
                        m.then_inc(w_used, 1)
                for s in range(TB):
                    turn(b, s)
                turned(b)
            up(i, "up", FC)
            g0 = gated_before(i, "up")
            down(i, "down", FC, lambda: pe.wait_ge(gated, g0 + FC))

    ctx.close()


def constants_of_the_shapes():
    c = np.zeros((P, C_ALL), np.float32)
    c[:, C_IDENT:C_IDENT + P] = np.eye(P)
    c[:, C_MASK:C_MASK + P] = np.where(np.arange(P)[None, :] > np.arange(P)[:, None], -1e30, 0.0)
    half = ROT // 2
    inv_freq = np.float32(500000.0) ** (-np.arange(0, ROT, 2, dtype=np.float32) / np.float32(ROT))
    angle = np.arange(SEQ, dtype=np.float32)[None, :] * inv_freq.astype(np.float32)[:, None]
    swap = np.arange(P)
    c[:, C_COS:C_COS + SEQ] = 1.0
    for m in range(2):
        r = m * HD
        swap[r:r + half], swap[r + half:r + ROT] = np.arange(r + half, r + ROT), np.arange(r, r + half)
        c[r:r + half, C_COS:C_COS + SEQ] = c[r + half:r + ROT, C_COS:C_COS + SEQ] = np.cos(angle)
        c[r:r + half, C_SIN:C_SIN + SEQ] = -np.sin(angle)
        c[r + half:r + ROT, C_SIN:C_SIN + SEQ] = np.sin(angle)
    c[swap, C_SWAP + np.arange(P)] = 1.0
    for g, w in enumerate(WINDOWS):
        c[:, C_COUNT + g * CMAX:C_COUNT + (g + 1) * CMAX] = 1.0 / np.minimum(np.arange(CMAX) + 1, w)
    c[:, C_ONES:C_ONES + P] = 1.0 / D
    return c


def kernel(**inputs):
    import concourse.bacc as bacc
    from concourse.bass_utils import run_bass_kernel_spmd

    a = {k: np.ascontiguousarray(v) for k, v in inputs.items()}
    at, n = column_layout()
    columns = np.zeros((P, n), np.float32)

    def put(name, j, v):
        v = v.reshape(-1, P).T
        columns[:, at[name, j]:at[name, j] + v.shape[1]] = v

    for j in range(a["attn_subln_g"].shape[0]):
        put("subln_g", j, a["attn_subln_g"][j])
    for j in range(a["conv_pw1_b"].shape[0]):
        put("pw1_b", j, a["conv_pw1_b"][j])
        put("dw_b", j, a["conv_dw_b"][j])
        put("cln_g", j, a["conv_ln_g"][j])
        put("cln_b", j, a["conv_ln_b"][j])
        taps = a["conv_dw_w"][j].reshape(CONV_W, KD, P).transpose(2, 1, 0)
        columns[:, at["dw_w", j]:at["dw_w", j] + CONV_W * KD] = taps.reshape(P, KD * CONV_W)

    send = {
        "x": a["x"][0], "wqkv": a["attn_wqkv"], "wo": a["attn_wo"], "lam": a["attn_lambda"].reshape(-1, 4 * HD),
        "pw1": a["conv_pw1_w"], "pw2": a["conv_pw2_w"], "pw2_b": a["conv_pw2_b"],
        "pool_w": a["pool_w"], "pool_b": a["pool_b"], "pool_s": a["pool_scale"],
        "w13": a["ffn_w13"], "w2": a["ffn_w2"],
        "g1": a["ln1_g"], "b1": a["ln1_b"], "g2": a["ln2_g"], "b2": a["ln2_b"],
        "columns": columns, "constants": constants_of_the_shapes(),
    }
    nc = bacc.Bacc("TRN2", target_bir_lowering=False, num_devices=1)
    aps, arrays = {}, {}
    for name, v in send.items():
        arrays[f"in_{name}"] = np.ascontiguousarray(v)
        aps[name] = nc.dram_tensor(f"in_{name}", v.shape, mybir.dt.from_np(v.dtype), kind="ExternalInput").ap()
    out = nc.dram_tensor("out", (SEQ, D), mybir.dt.float32, kind="ExternalOutput").ap()
    build(nc, out=out, **aps)
    r = run_bass_kernel_spmd(nc, [arrays], core_ids=[0])
    return r.results[0]["out"].reshape(1, SEQ, D)
```
